# Optimizing a Trainium2 kernel written in Bass

```python
import jax, jax.numpy as jnp
from jax import lax
import numpy as np

D_MODEL = 2048
BATCH = 1
SEQ = 256
DEPTH = 2

HEAD_DIM = 128
N_Q_HEADS = 8
N_KV_HEADS = 2
GQA_GROUP = N_Q_HEADS // N_KV_HEADS
N_MEM_HEADS = 4
MEM_TOKENS = 256
SGU_GROUPS = 4
SGU_CHUNK = 128
Q_BLOCK = 128
GRID_W = 64
ROPE_THETA = 10000.0
N_BRANCH = 3
EPS = 1e-6
D_FF = -(-8 * D_MODEL // (3 * 256)) * 256

SGU_WIDTH = SGU_GROUPS * HEAD_DIM
Q_WIDTH = N_Q_HEADS * HEAD_DIM
KV_WIDTH = N_KV_HEADS * HEAD_DIM
MEM_WIDTH = N_MEM_HEADS * HEAD_DIM
GATE_WIDTH = N_BRANCH * D_MODEL
IN_WIDTH = 2 * SGU_WIDTH + Q_WIDTH + 2 * KV_WIDTH + MEM_WIDTH + GATE_WIDTH
SPLIT_IDX = [2 * SGU_WIDTH,
             2 * SGU_WIDTH + Q_WIDTH,
             2 * SGU_WIDTH + Q_WIDTH + KV_WIDTH,
             2 * SGU_WIDTH + Q_WIDTH + 2 * KV_WIDTH,
             2 * SGU_WIDTH + Q_WIDTH + 2 * KV_WIDTH + MEM_WIDTH]

kernel_name = "hybrid_gated_sgu_gqa_memxattn_encoder"

def rms_norm(x, g):
    xf = x.astype(jnp.float32)
    y = xf * lax.rsqrt(jnp.mean(xf * xf, axis=-1, keepdims=True) + EPS)
    return (y * g.astype(jnp.float32)).astype(x.dtype)

def axial_rope_tables(rows):
    half = HEAD_DIM // 2
    inv = ROPE_THETA ** (-jnp.arange(0, half, 2, dtype=jnp.float32) / half)
    r = jnp.repeat(jnp.arange(rows, dtype=jnp.float32), GRID_W)
    c = jnp.tile(jnp.arange(GRID_W, dtype=jnp.float32), rows)
    ar = r[:, None] * inv[None, :]
    ac = c[:, None] * inv[None, :]
    return (jnp.cos(ar), jnp.sin(ar), jnp.cos(ac), jnp.sin(ac))

def rotate(x, cos, sin):
    x1, x2 = jnp.split(x, 2, axis=-1)
    cos = cos.astype(x.dtype)
    sin = sin.astype(x.dtype)
    return jnp.concatenate([x1 * cos - x2 * sin, x2 * cos + x1 * sin], axis=-1)

def apply_axial_rope(x, tabs):
    cos_r, sin_r, cos_c, sin_c = tabs
    half = HEAD_DIM // 2
    return jnp.concatenate([rotate(x[..., :half], cos_r, sin_r),
                            rotate(x[..., half:], cos_c, sin_c)], axis=-1)

def block_gqa(q, k, v):
    B, KV, G, S, Dh = q.shape
    nb = S // Q_BLOCK
    qb = q.reshape(B, KV, G, nb, Q_BLOCK, Dh).transpose(3, 0, 1, 2, 4, 5)
    scale = Dh ** -0.5

    def one_block(qblk):
        s = jnp.einsum('bkgqd,bksd->bkgqs', qblk, k).astype(jnp.float32) * scale
        p = jax.nn.softmax(s, axis=-1).astype(v.dtype)
        return jnp.einsum('bkgqs,bksd->bkgqd', p, v)

    o = lax.map(one_block, qb)
    return o.transpose(1, 2, 3, 0, 4, 5).reshape(B, KV, G, S, Dh)

def hybrid_layer(x, mem, tabs, norm_mix, w_in, gate_b, sgu_norm, sgu_w, sgu_b,
                 q_norm, k_norm, mem_norm, w_mem_kv, mq_norm, mk_norm,
                 w_br_sgu, w_br_attn, w_br_mem, w_out, norm_ffn, w_gate_up, w_down):
    B, S, D = x.shape
    M = mem.shape[1]
    h = rms_norm(x, norm_mix)
    z = h @ w_in
    z_sgu, zq, zk, zv, zmq, zg = jnp.split(z, SPLIT_IDX, axis=-1)

    zs = jax.nn.gelu(z_sgu, approximate=False)
    u, vs = jnp.split(zs, 2, axis=-1)
    vs = rms_norm(vs.reshape(B, S, SGU_GROUPS, HEAD_DIM), sgu_norm)
    vc = vs.reshape(B, S // SGU_CHUNK, SGU_CHUNK, SGU_GROUPS, HEAD_DIM)
    sp = jnp.einsum('gpq,bnqgc->bnpgc', sgu_w, vc) + sgu_b.T[None, None, :, :, None]
    y_sgu = u * sp.reshape(B, S, SGU_WIDTH)

    q = zq.reshape(B, S, N_Q_HEADS, HEAD_DIM).transpose(0, 2, 1, 3)
    k = zk.reshape(B, S, N_KV_HEADS, HEAD_DIM).transpose(0, 2, 1, 3)
    v = zv.reshape(B, S, N_KV_HEADS, HEAD_DIM).transpose(0, 2, 1, 3)
    q = apply_axial_rope(rms_norm(q, q_norm), tabs)
    k = apply_axial_rope(rms_norm(k, k_norm), tabs)
    o = block_gqa(q.reshape(B, N_KV_HEADS, GQA_GROUP, S, HEAD_DIM), k, v)
    y_attn = o.reshape(B, N_Q_HEADS, S, HEAD_DIM).transpose(0, 2, 1, 3).reshape(B, S, Q_WIDTH)

    mkv = rms_norm(mem, mem_norm) @ w_mem_kv
    mk, mv = jnp.split(mkv, 2, axis=-1)
    mk = rms_norm(mk.reshape(B, M, N_MEM_HEADS, HEAD_DIM), mk_norm).transpose(0, 2, 1, 3)
    mv = mv.reshape(B, M, N_MEM_HEADS, HEAD_DIM).transpose(0, 2, 1, 3)
    mq = rms_norm(zmq.reshape(B, S, N_MEM_HEADS, HEAD_DIM), mq_norm).transpose(0, 2, 1, 3)
    ms = jnp.einsum('bhqd,bhmd->bhqm', mq, mk).astype(jnp.float32) * (HEAD_DIM ** -0.5)
    mp = jax.nn.softmax(ms, axis=-1).astype(mv.dtype)
    mo = jnp.einsum('bhqm,bhmd->bhqd', mp, mv)
    y_mem = mo.transpose(0, 2, 1, 3).reshape(B, S, MEM_WIDTH)

    g = jax.nn.sigmoid((zg.reshape(B, S, N_BRANCH, D) + gate_b).astype(jnp.float32)).astype(x.dtype)
    y = (g[:, :, 0] * (y_sgu @ w_br_sgu)
         + g[:, :, 1] * (y_attn @ w_br_attn)
         + g[:, :, 2] * (y_mem @ w_br_mem))
    x = x + y @ w_out

    a, b = jnp.split(rms_norm(x, norm_ffn) @ w_gate_up, 2, axis=-1)
    return x + (jax.nn.silu(a) * b) @ w_down

def setup_inputs(seed: int = 0) -> dict:
    key = jax.random.key(seed)
    ks = jax.random.split(key, 24)
    f32 = jnp.float32

    def nrm(k, shape, fan_in):
        return jax.random.normal(k, shape, f32) * (fan_in ** -0.5)

    def gain(k, shape):
        return 1.0 + 0.05 * jax.random.normal(k, shape, f32)

    L = DEPTH
    return {
        "x": jax.random.normal(ks[0], (BATCH, SEQ, D_MODEL), f32),
        "mem": jax.random.normal(ks[1], (BATCH, MEM_TOKENS, D_MODEL), f32),
        "norm_mix": gain(ks[2], (L, D_MODEL)),
        "w_in": nrm(ks[3], (L, D_MODEL, IN_WIDTH), D_MODEL),
        "gate_b": 0.01 * jax.random.normal(ks[4], (L, N_BRANCH, D_MODEL), f32),
        "sgu_norm": gain(ks[5], (L, HEAD_DIM)),
        "sgu_w": nrm(ks[6], (L, SGU_GROUPS, SGU_CHUNK, SGU_CHUNK), SGU_CHUNK),
        "sgu_b": 1.0 + 0.05 * jax.random.normal(ks[7], (L, SGU_GROUPS, SGU_CHUNK), f32),
        "q_norm": gain(ks[8], (L, HEAD_DIM)),
        "k_norm": gain(ks[9], (L, HEAD_DIM)),
        "mem_norm": gain(ks[10], (L, D_MODEL)),
        "w_mem_kv": nrm(ks[11], (L, D_MODEL, 2 * MEM_WIDTH), D_MODEL),
        "mq_norm": gain(ks[12], (L, HEAD_DIM)),
        "mk_norm": gain(ks[13], (L, HEAD_DIM)),
        "w_br_sgu": nrm(ks[14], (L, SGU_WIDTH, D_MODEL), SGU_WIDTH),
        "w_br_attn": nrm(ks[15], (L, Q_WIDTH, D_MODEL), Q_WIDTH),
        "w_br_mem": nrm(ks[16], (L, MEM_WIDTH, D_MODEL), MEM_WIDTH),
        "w_out": nrm(ks[17], (L, D_MODEL, D_MODEL), D_MODEL),
        "norm_ffn": gain(ks[18], (L, D_MODEL)),
        "w_gate_up": nrm(ks[19], (L, D_MODEL, 2 * D_FF), D_MODEL),
        "w_down": nrm(ks[20], (L, D_FF, D_MODEL), D_FF),
    }

def reference(x, mem, norm_mix, w_in, gate_b, sgu_norm, sgu_w, sgu_b, q_norm, k_norm,
              mem_norm, w_mem_kv, mq_norm, mk_norm, w_br_sgu, w_br_attn, w_br_mem,
              w_out, norm_ffn, w_gate_up, w_down):
    rows = x.shape[1] // GRID_W
    tabs = axial_rope_tables(rows)
    for l in range(DEPTH):
        x = hybrid_layer(x, mem, tabs, norm_mix[l], w_in[l], gate_b[l], sgu_norm[l], sgu_w[l],
                         sgu_b[l], q_norm[l], k_norm[l], mem_norm[l], w_mem_kv[l], mq_norm[l],
                         mk_norm[l], w_br_sgu[l], w_br_attn[l], w_br_mem[l], w_out[l],
                         norm_ffn[l], w_gate_up[l], w_down[l])
    return x


_drawn_inputs = setup_inputs


def setup_inputs(seed=0):
    import zlib

    import numpy as np

    out = dict(_drawn_inputs(seed))
    spreads = {}
    factors = {'gate_b': 8.0,
     'q_norm': 8.0,
     'k_norm': 8.0,
     'mem_norm': 8.0,
     'mq_norm': 8.0,
     'mk_norm': 8.0}
    for name, (base, spread) in spreads.items():
        noise = np.random.default_rng([zlib.crc32(name.encode()), seed]).standard_normal(out[name].shape)
        drawn = base * np.exp(spread * noise) if base else spread * noise
        out[name] = __import__('jax').numpy.asarray(drawn.astype(out[name].dtype))
    for name, factor in factors.items():
        out[name] = (out[name] * factor).astype(out[name].dtype)
    return out
```

```python
from contextlib import ExitStack, contextmanager

import numpy as np

import concourse.bass as bass
from concourse import mybir

F32 = mybir.dt.float32
F32R = mybir.dt.float32r
I32 = mybir.dt.int32
ALU = mybir.AluOpType
ACT = mybir.ActivationFunctionType
AX_X = mybir.AxisListType.X

P = 128
DEPTH = 2
D = 2048
SEQ = 256
TB = SEQ // P
HD = 128
N_Q, N_KV, N_MEM = 8, 2, 4
GROUP = N_Q // N_KV
N_HEADS = N_MEM + N_Q
SGU_G = 4
D_FF = 5632
N_BRANCH = 3
EPS = 1e-6
GRID_W = 64
ROPE_THETA = 10000.0
SCALE = float(HD) ** -0.5

COLS = 512
KT = D // P
UNIT_KT = 4
HALF_KT = 2
UNIT = UNIT_KT * COLS
HALF = HALF_KT * COLS
NC = D // COLS
FULL = KT // HALF_KT
RAW_SLOTS = 4
MEM_KT = KT // RAW_SLOTS
DMA_RING = 2048
SPLIT_SLOTS = 4
LEAD = SPLIT_SLOTS - 1
ACT_GROUPS = D_FF // COLS
PART = 4
LAST = ACT_GROUPS - 2 * PART
SEED = float(0x5F3759DF)


def units_of(w, chunk):
    k = w.shape[0] // (UNIT_KT * P)
    return (w[:, chunk * COLS:(chunk + 1) * COLS].reshape(k, UNIT_KT, P, COLS)
            .transpose(0, 2, 1, 3).reshape(k, P, UNIT))


def layer_stream(w_in, w_mem, w_sgu, w_attn, w_mbr, w_out, w_gu, w_down):
    z = [0, 1, 4, 5, 2, 3]
    g = [[(w_in, len(z) + NC * b + c) for c in range(NC)] for b in range(N_BRANCH)]
    order = [(w_mem, 0), (w_mem, 1)] + [(w_in, c) for c in z] + g[0] + [g[1][0]]
    for c in range(NC):
        order += [g[2][c], (w_sgu, c), (w_mbr, c), (w_attn, c)]
        if c + 1 < NC:
            order.append(g[1][c + 1])
    order += [(w_out, c) for c in range(NC)]
    a, b = [(w_gu, j) for j in range(ACT_GROUPS)], [(w_gu, ACT_GROUPS + j) for j in range(ACT_GROUPS)]
    order.append(a[0])
    for j0, n in ((0, PART), (PART, PART), (2 * PART, LAST)):
        rows = w_down[j0 * COLS:(j0 + n) * COLS]
        for j in range(j0, j0 + n):
            order.append(b[j])
            if j + 1 < j0 + n:
                order.append(a[j + 1])
        order += [(rows, c) for c in range(NC)]
        if j0 + n < ACT_GROUPS:
            order.append(a[j0 + n])
    return order


N_UNITS = (2 * KT + 6 * KT + 3 * NC * KT + NC * (4 + 4 + 8) + NC * KT + 2 * ACT_GROUPS * KT
           + NC * D_FF // P) // UNIT_KT
V_MEM, V_MIX, V_FFN, V_MQ, V_MK, V_SGUB = 0, KT, 2 * KT, 3 * KT, 3 * KT + 1, 3 * KT + 2
N_VEC = V_SGUB + SGU_G
OPS_LAYER = KT // HALF_KT + NC + 1 + N_HEADS + NC + NC + ACT_GROUPS


class Counts:

    def __init__(self, eng):
        self.eng, self.n, self.loops = eng, {}, []

    def add(self, name, k=1):
        self.n[name] = self.n.get(name, 0) + k

    def at(self, name, more=0, times=1):
        value = (self.n.get(name, 0) + more) if times == 1 else self.n.get(name, 0) * times + more
        for var, per_turn in self.loops:
            if per_turn.get(name):
                value = var * (per_turn[name] * times) + value
        return value

    @contextmanager
    def loop(self, turns, **per_turn):
        before = dict(self.n)
        with self.eng.Fori(0, turns) as i:
            self.loops.append((i, per_turn))
            yield i
            self.loops.pop()
        for name in set(self.n) | set(per_turn):
            got = self.n.get(name, 0) - before.get(name, 0)
            assert got == per_turn.get(name, 0), (name, got, per_turn.get(name, 0))
            self.n[name] = before.get(name, 0) + turns * per_turn.get(name, 0)


def trunk(nc, weights, x_in, mem_in, memT_in, vecs_in, gains_in, sguT_in, rope_in, bias_in, out):
    with ExitStack() as ctx:
        def sb(name, shape, dt=F32):
            return ctx.enter_context(nc.sbuf_tensor(name, shape, dt))

        def psum(name, shape):
            return ctx.enter_context(nc.psum_tensor(name, shape, F32))

        def sem(name):
            return ctx.enter_context(nc.semaphore(name))

        raw = sb("raw", [P, RAW_SLOTS, UNIT])
        w_hi = sb("w_hi", [P, SPLIT_SLOTS, HALF], F32R)
        w_lo = sb("w_lo", [P, SPLIT_SLOTS, HALF], F32R)
        a_hi = sb("a_hi", [P, KT, SEQ], F32R)
        a_lo = sb("a_lo", [P, KT, SEQ], F32R)
        b_hi = sb("b_hi", [P, KT, SEQ], F32R)
        b_lo = sb("b_lo", [P, KT, SEQ], F32R)
        x = sb("x", [P, TB, D])
        y = sb("y", [P, TB * D])
        rows = sb("rows", [P, 6, TB, COLS])
        mem_v = sb("mem_v", [P, TB, COLS])
        mem_kT = sb("mem_kT", [P, N_MEM, SEQ])
        mem_qT = sb("mem_qT", [P, N_MEM, SEQ])
        kT = sb("kT", [P, N_KV, SEQ])
        qT = sb("qT", [P, N_Q, SEQ])
        prob_b = sb("prob_b", [P, TB, SEQ])
        rope = sb("rope", [P, 2, TB, HD])
        turn = sb("turn", [P, 4, TB, HD])
        vecs_all = sb("vecs_all", [P, DEPTH, N_VEC])
        vecs = sb("vecs", [P, N_VEC])
        ident = sb("ident", [P, P])
        bias = sb("bias", [P, 2, COLS])
        stats = sb("stats", [P, 112])

        R_U, R_V, R_KV, R_MQ, R_Q = 0, 1, 2, 3, 4
        R_MK, R_TMP = R_Q, R_Q + 1
        y_rows = y[:, :].rearrange("p (t n) -> p t n", t=TB)
        memT = y[:, :].rearrange("p (k s) -> p k s", k=KT)
        mem_rows = rows[:, 0:4, :, :].rearrange("p a t n -> p (a t n)").rearrange("p (t n) -> p t n", t=TB)
        v_rows = rows[:, R_KV, :, N_KV * HD:COLS]
        sguT = qT[:, 0:2, :].rearrange("p a b -> p (a b)")
        gains = qT[:, 2:4, :].rearrange("p a b -> p (a b)")[:, 0:3 * HD]

        rs_mem, rs_x, rs_ffn = stats[:, 0:2], stats[:, 2:4], stats[:, 4:6]
        ss_mem, ss_x, ss_sum = stats[:, 6:8], stats[:, 8:10], stats[:, 10:12]
        ss_ffn = stats[:, 12:20].rearrange("p (t c) -> p t c", t=TB)
        ss, rs, newton, guess = stats[:, 20:28], stats[:, 28:36], stats[:, 36:44], stats[:, 44:52]
        q_scale = stats[:, 52:76].rearrange("p (g t h) -> p g t h", g=3, t=TB)
        top = stats[:, 76:80].rearrange("p (b t) -> p b t", t=TB)
        low = stats[:, 80:84].rearrange("p (b t) -> p b t", t=TB)
        den = stats[:, 84:88].rearrange("p (b t) -> p b t", t=TB)
        inv = stats[:, 88:92].rearrange("p (b t) -> p b t", t=TB)

        acc = [psum(f"acc{i}", [P, TB, COLS]) for i in range(3)]
        tr = psum("tr", [P, 4, SEQ])
        scores = acc[2]
        pT_ps = tr[:, 0:2, :]
        oT_ps = tr[:, 2:4, :]

        raw_loaded = [sem(f"raw_loaded{s}") for s in range(RAW_SLOTS)]
        hi_ready, lo_ready, half_used = sem("hi_ready"), sem("lo_ready"), sem("half_used")
        taken = [sem(f"taken{i}") for i in range(3)]
        tr_done, tr_free = sem("tr_done"), sem("tr_free")
        op_hi = sem("op_hi")
        mem_ready, head_ready = sem("mem_ready"), sem("head_ready")
        rows_ready = sem("rows_ready")
        sig_ready = sem("sig_ready")
        sgu_done, sums_done, rs_ready = sem("sgu_done"), sem("sums_done"), sem("rs_ready")
        mem_loaded = [sem(f"mem_loaded{s}") for s in range(RAW_SLOTS)]
        x_loaded, memrow_loaded = sem("x_loaded"), sem("memrow_loaded")
        vecs_loaded, rope_loaded, layer_loaded = sem("vecs_loaded"), sem("rope_loaded"), sem("layer_loaded")
        bias_loaded, bias_used = [sem("bias_loaded0"), sem("bias_loaded1")], sem("bias_used")
        vecs_ready, ident_ready = sem("vecs_ready"), sem("ident_ready")
        scored, low_ready, exp_done = sem("scored"), sem("low_ready"), sem("exp_done")
        inv_ready, prob_ready = sem("inv_ready"), sem("prob_ready")
        pT_done, pT_ready, oT_done = sem("pT_done"), sem("pT_ready"), sem("oT_done")
        stored, x_final = sem("stored"), sem("x_final")
        load_step = sem("load_step")

        def prob(a):
            return rows[:, R_U, :, 0:SEQ] if a % 2 == 0 else prob_b[:, :, :]

        def probT(a):
            return rows[:, R_MQ, a % 2, :].rearrange("p (k s) -> p k s", k=TB)

        def head_kt(a):
            return SGU_G + a

        def columns(c):
            return slice(c * COLS, (c + 1) * COLS) if isinstance(c, int) else bass.ds(c * COLS, COLS)

        def kts(j):
            return slice(4 * j, 4 * j + 4) if isinstance(j, int) else bass.ds(j * 4, 4)

        block = ctx.enter_context(nc.Block())

        @block.sync
        def _(sp):
            stream = weights.rearrange("l u p n -> (l u) p n")
            sp.dma_start(vecs_all[:, :, :], vecs_in).then_inc(vecs_loaded, 16)
            for s in range(RAW_SLOTS):
                if s > 0:
                    sp.wait_ge(mem_loaded[s - 1], 16)
                if s == RAW_SLOTS - 1:
                    sp.dma_start(x[:, :, :], x_in.rearrange("b (t p) d -> p (b t) d", p=P)).then_inc(x_loaded, 16)
                sp.dma_start(raw[:, s, :], stream[s]).then_inc(raw_loaded[s], 16)
            with sp.Fori(1, DEPTH * N_UNITS // RAW_SLOTS) as i:
                for s in range(RAW_SLOTS):
                    sp.wait_ge(lo_ready, i * (2 * RAW_SLOTS) + (2 * s + 2))
                    sp.dma_start(raw[:, s, :], stream[i * RAW_SLOTS + s]).then_inc(raw_loaded[s], 16)
            done = 1 + DEPTH * ACC_LAYER
            for c, (s, value) in enumerate(((taken[0], done - 1), (taken[1], done), (taken[0], done), (x_final, 1))):
                sp.wait_ge(s, value)
                sp.dma_start(out.rearrange("b (t p) d -> p (b t) d", p=P)[:, :, columns(c)], x[:, :, columns(c)]
                             ).then_inc(stored, 16)
            sp.wait_ge(stored, 16 * NC)

        @block.gpsimd
        def _(pool):
            n = Counts(pool)
            def load_memory():
                for s in range(RAW_SLOTS):
                    kt = slice(s * MEM_KT, (s + 1) * MEM_KT)
                    pool.dma_start(memT[:, kt, :], memT_in[:, kt, :]).then_inc(mem_loaded[s], 16)

            load_memory()
            pool.memset(prob_b[:, :, :], 0.0).then_inc(ident_ready, 1)
            pool.memset(ident[:, :], 0.0).then_inc(ident_ready, 1)
            pool.wait_ge(ident_ready, 2)
            pool.affine_select(out=ident[:, :], in_=ident[:, :], compare_op=ALU.not_equal, fill=1.0,
                               base=0, pattern=[[-1, P]], channel_multiplier=1).then_inc(ident_ready, 1)

            def load_bias(k, layer):
                pool.wait_ge(bias_used, n.at("bias", 1))
                pool.sem_inc(load_step, 1)
                pool.dma_start(bias[:, k % 2, :], bias_in[layer, k:k + 1, :].to_broadcast([P, COLS])
                               ).then_inc(bias_loaded[k % 2], 16)
                n.add("bias")

            def scale_head(a):
                pool.wait_ge(inv_ready, n.at("head", 1))
                pool.tensor_tensor(prob(a), prob(a), inv[:, a % 2, :].unsqueeze(2).to_broadcast([P, TB, SEQ]),
                                   ALU.mult).then_inc(prob_ready, 1)
                n.add("head")

            pool.dma_start(rope[:, :, :, :], rope_in).then_inc(rope_loaded, 16)

            with n.loop(DEPTH, bias=N_BRANCH * NC, head=N_HEADS, tr=TR_LAYER, half=2 * N_UNITS) as layer:
                pool.wait_ge(half_used, n.at("half", SPLIT_SLOTS))
                pool.sem_inc(load_step, 1)
                pool.dma_start(mem_rows, mem_in.rearrange("b (t p) d -> p (b t) d", p=P)).then_inc(memrow_loaded, 16)
                pool.wait_ge(scored, n.at("head", 1))
                pool.sem_inc(load_step, 1)
                pool.dma_start(sguT, sguT_in[layer]).then_inc(layer_loaded, 16)
                pool.dma_start(gains, gains_in[layer].to_broadcast([P, 3 * HD])).then_inc(layer_loaded, 16)
                load_bias(0, layer)
                load_bias(1, layer)
                for a in range(N_HEADS):
                    scale_head(a)
                    if a in (3, 7, 11):
                        load_bias(2 + a // 4, layer)
                for k in range(5, N_BRANCH * NC):
                    load_bias(k, layer)
                n.add("tr", TR_Y)
                pool.wait_ge(tr_done, n.at("tr"))
                pool.sem_inc(load_step, 1)
                load_memory()
                n.add("tr", TR_LAYER - TR_Y)
                n.add("half", 2 * N_UNITS)
            for s in mem_loaded:
                pool.wait_ge(s, 16 * (DEPTH + 1))

        @block.tensor
        def _(pe):
            n = Counts(pe)
            A, B = (a_hi, a_lo), (b_hi, b_lo)

            def half(acc_i, hi, lo, kt, first, last):
                pe.wait_ge(lo_ready, n.at("half", 2 * RAW_SLOTS + 1))
                slot = n.n.get("half", 0) % SPLIT_SLOTS
                for k in range(HALF_KT):
                    wh = w_hi[:, slot, k * COLS:(k + 1) * COLS]
                    wl = w_lo[:, slot, k * COLS:(k + 1) * COLS]
                    for t in range(TB):
                        o = acc[acc_i][:, t, :]
                        tok = slice(t * P, (t + 1) * P)
                        pe.matmul(o, hi[:, kt + k, tok], wh, start=first and k == 0, stop=False)
                        pe.matmul(o, hi[:, kt + k, tok], wl, start=False, stop=False)
                        mm = pe.matmul(o, lo[:, kt + k, tok], wh, start=False, stop=last and k == HALF_KT - 1)
                mm.then_inc(half_used, 1)
                n.add("half")

            def chunk(acc_i, hi, lo, halves=FULL, kt=0, first=0, upto=None, need=()):
                if first == 0:
                    pe.wait_ge(taken[acc_i], n.at(f"acc{acc_i}", 1))
                    n.add(f"acc{acc_i}")
                for h in range(first, halves if upto is None else upto):
                    if h in need:
                        pe.wait_ge(tr_free, n.at("tr", 1 - need[h]))
                    half(acc_i, hi, lo, kt + h * HALF_KT, h == 0, h == halves - 1)

            def transposes(src, blocks=4):
                pe.wait_ge(tr_free, n.at("tr", 1))
                for b in range(blocks):
                    for t in range(TB):
                        tp = pe.transpose(tr[:, b, t * P:(t + 1) * P], src(b, t), ident[:, :])
                tp.then_inc(tr_done, 1)
                n.add("tr")

            def rows_at(r):
                return lambda b, t: rows[:, r, t, b * HD:(b + 1) * HD]

            def x_at(c):
                return lambda b, t: x[:, t, c * COLS + b * P:c * COLS + (b + 1) * P]

            def y_at(c):
                return lambda b, t: y_rows[:, t, c * COLS + b * P:c * COLS + (b + 1) * P]

            def wait_rows():
                n.add("rows")
                pe.wait_ge(rows_ready, n.at("rows"))

            def wait_taken(acc_i):
                pe.wait_ge(taken[acc_i], n.at(f"acc{acc_i}", 1))

            def head_scores(a):
                if a >= 2:
                    pe.wait_ge(exp_done, n.at("head", -1))
                for t in range(TB):
                    tok = slice(t * P, (t + 1) * P)
                    if a < N_MEM:
                        q_, k_ = mem_qT[:, a, tok], mem_kT[:, a, :]
                    else:
                        q_, k_ = qT[:, a - N_MEM, tok], kT[:, (a - N_MEM) // GROUP, :]
                    mm = pe.matmul(scores[:, a % 2, t * SEQ:(t + 1) * SEQ], q_, k_, start=True, stop=True)
                mm.then_inc(scored, 1)
                n.add("head")

            def head_turn(a):
                pe.wait_ge(prob_ready, n.at("turned", 1))
                if a == 0:
                    pe.wait_ge(tr_free, n.at("tr", 1))
                else:
                    pe.wait_ge(pT_ready, n.at("turned"))
                for k in range(TB):
                    for t in range(TB):
                        tp = pe.transpose(pT_ps[:, k, t * P:(t + 1) * P], prob(a)[:, t, k * P:(k + 1) * P],
                                          ident[:, :])
                tp.then_inc(pT_done, 1)
                n.add("turned")

            def head_values(a):
                pe.wait_ge(pT_ready, n.at("valued", 1))
                if a >= 1:
                    pe.wait_ge(head_ready, n.at("valued"))
                for k in range(TB):
                    if a < N_MEM:
                        v_ = mem_v[:, k, a * HD:(a + 1) * HD]
                    else:
                        kv = (a - N_MEM) // GROUP
                        v_ = v_rows[:, k, kv * HD:(kv + 1) * HD]
                    mm = pe.matmul(oT_ps[:, a % 2, :], v_, probT(a)[:, k, :], start=k == 0, stop=k == TB - 1)
                mm.then_inc(oT_done, 1)
                n.add("valued")

            pe.wait_ge(ident_ready, 3)
            for t in range(TB):
                zeros = prob_b[:, :, :].rearrange("p t n -> p (t n)")
                mm = pe.matmul(acc[1][:, t, :], zeros[:, 0:P], zeros, start=True, stop=True)
            mm.then_inc(half_used, SPLIT_SLOTS)
            n.add("acc1")

            with n.loop(DEPTH, half=2 * N_UNITS, tr=TR_LAYER, rows=ROWS_LAYER, acc0=ACC_LAYER, acc1=ACC_LAYER,
                        acc2=NC, head=N_HEADS, turned=N_HEADS, valued=N_HEADS, mem=FULL):
                for h in range(FULL):
                    n.add("mem")
                    pe.wait_ge(mem_ready, n.at("mem"))
                    chunk(0, *B, first=h, upto=h + 1)
                    if h == 6:
                        wait_taken(1)
                        transposes(x_at(0))
                for h in range(FULL):
                    chunk(1, *B, first=h, upto=h + 1)
                    if h in (0, 2, 4):
                        transposes(x_at(1 + h // 2))
                chunk(0, *A, upto=1, need={0: 3})
                wait_rows()
                transposes(rows_at(R_MK))
                chunk(0, *A, first=1, need={2: 3, 4: 2, 6: 1})
                chunk(1, *A)
                chunk(0, *A, upto=6)
                wait_rows()
                for g in range(SGU_G):
                    mm = pe.matmul(acc[2][:, g // 2, g % 2 * SEQ:(g % 2 + 1) * SEQ],
                                   sguT[:, g * P:(g + 1) * P], rows[:, R_V, :, g * HD:(g + 1) * HD],
                                   start=True, stop=True)
                mm.then_inc(sgu_done, 1)
                chunk(0, *A, first=6)
                chunk(1, *A, upto=1)
                wait_rows()
                transposes(rows_at(R_U))
                chunk(1, *A, first=1)
                chunk(0, *A, upto=2)
                wait_rows()
                transposes(rows_at(R_KV), N_KV)
                chunk(0, *A, first=2, upto=4)
                wait_taken(1)
                transposes(rows_at(R_MQ))
                chunk(0, *A, first=4)
                chunk(1, *A, upto=7)
                wait_rows()
                transposes(rows_at(R_Q))
                chunk(1, *A, first=7)
                for i in range(NC * UNIT_KT):
                    for h in range(i % 4 * 2, i % 4 * 2 + 2):
                        chunk(i // 4 % 2, *A, first=h, upto=h + 1)
                        if i == 3 and h == 6:
                            wait_rows()
                            transposes(rows_at(R_Q + 1))
                    if 0 <= i - 1 < N_HEADS:
                        head_scores(i - 1)
                    if 0 <= i - 3 < N_HEADS:
                        head_turn(i - 3)
                    if 0 <= i - 4 < N_HEADS:
                        head_values(i - 4)
                chunk(0, *A, upto=FULL - 1)
                pe.wait_ge(head_ready, n.at("valued"))
                pe.wait_ge(exp_done, n.at("head"))
                chunk(0, *A, first=FULL - 1)
                with n.loop(NC - 1, half=HALVES_Y, acc0=2, acc1=2, acc2=1, rows=1):
                    chunk(1, *A)
                    chunk(0, *B, halves=2)
                    chunk(1, *B, halves=2, kt=4)
                    chunk(2, *B, halves=4, kt=8)
                    chunk(0, *A)
                    n.add("rows")
                chunk(1, *A)
                chunk(0, *B, halves=2)
                pe.wait_ge(rows_ready, n.at("rows"))
                transposes(y_at(0))
                chunk(1, *B, halves=2, kt=4)
                transposes(y_at(1))
                chunk(2, *B, halves=4, kt=8, upto=2)
                transposes(y_at(2))
                chunk(2, *B, halves=4, kt=8, first=2)
                chunk(0, *B, upto=3, need={0: 2, 2: 1})
                wait_rows()
                transposes(y_at(NC - 1))
                chunk(0, *B, first=3, need={4: 1, 6: 0})
                for c in range(1, NC):
                    chunk(c % 2, *B, upto=2)
                    wait_taken((c - 1) % 2)
                    transposes(x_at(c - 1))
                    chunk(c % 2, *B, first=2)

                chunk(0, *A, upto=2, need={0: 2})
                wait_taken((NC - 1) % 2)
                transposes(x_at(NC - 1))
                chunk(0, *A, first=2, need={2: 2, 4: 1, 6: 0})

                def inner(groups):
                    with n.loop(groups - 1, half=2 * FULL, acc0=1, acc1=1, tr=1):
                        chunk(1, *A)
                        chunk(0, *A, upto=2)
                        wait_taken(1)
                        transposes(rows_at(R_MQ))
                        chunk(0, *A, first=2)
                    chunk(1, *A)

                def down(groups):
                    halves = 2 * groups
                    chunk(0, *B, halves=halves, upto=2, need={0: 0})
                    wait_taken(1)
                    transposes(rows_at(R_MQ))
                    chunk(0, *B, halves=halves, first=2, need={halves - 2: 0})
                    for c in range(1, NC):
                        chunk(c % 2, *B, halves=halves)

                with n.loop(2, half=2 * PART * FULL + NC * 2 * PART, acc0=PART + 2, acc1=PART + 2, tr=PART):
                    inner(PART)
                    down(PART)
                    chunk(0, *A)
                inner(LAST)
                down(LAST)

        @block.scalar
        def _(act):
            n = Counts(act)

            def split(halves):
                for _ in range(halves):
                    h = n.n.get("half", 0)
                    slot, part = h // 2 % RAW_SLOTS, h % 2
                    if part == 0:
                        act.wait_ge(raw_loaded[slot], n.at("half", 16 - 4 * slot, 2))
                    act.wait_ge(half_used, n.at("half", 1))
                    act.activation(w_hi[:, h % SPLIT_SLOTS, :], raw[:, slot, part * HALF:(part + 1) * HALF],
                                   ACT.Copy).then_inc(hi_ready, 1)
                    n.add("half")

            def chunk_done(lead):
                act.wait_ge(half_used, n.at("half", SPLIT_SLOTS - lead))

            def wait_tr():
                n.add("tr")
                act.wait_ge(tr_done, n.at("tr"))

            def op_gain(hi, kt0, gain):
                wait_tr()
                for k in range(kt0, kt0 + 4):
                    last = act.activation(hi[:, k, :], tr[:, k - kt0, :], ACT.Copy,
                                          scale=vecs[:, gain + k:gain + k + 1])
                last.then_inc(op_hi, 1)

            def op_plain(hi):
                wait_tr()
                act.activation(hi, tr[:, :, :], ACT.Copy).then_inc(op_hi, 1)

            def turn_out(dst, scale=1.0, blocks=4):
                wait_tr()
                act.activation(dst, tr[:, 0:blocks, :], ACT.Copy, scale=scale).then_inc(tr_free, 1)

            def take_out(acc_i, r, func):
                chunk_done(4)
                for t in range(TB):
                    last = act.activation(rows[:, r, t, :], acc[acc_i][:, t, :], func, scale=rs_x[:, t:t + 1])
                last.then_inc(taken[acc_i], 1)
                n.add(f"acc{acc_i}")

            def wait_taken(acc_i):
                n.add(f"acc{acc_i}")
                act.wait_ge(taken[acc_i], n.at(f"acc{acc_i}", 1))

            def head_exp(a):
                act.wait_ge(low_ready, n.at("head", 1))
                if a >= 2:
                    act.wait_ge(pT_done, n.at("head", -1))
                for t in range(TB):
                    last = act.activation(prob(a)[:, t, :], scores[:, a % 2, t * SEQ:(t + 1) * SEQ], ACT.Exp,
                                          bias=low[:, a % 2, t:t + 1],
                                          scale=q_scale[:, a // 4, t, a % 4:a % 4 + 1],
                                          accum_out=den[:, a % 2, t:t + 1])
                last.then_inc(exp_done, 1)
                n.add("head")

            def head_pT(a):
                act.wait_ge(pT_done, n.at("pT", 1))
                if a >= 2:
                    act.wait_ge(oT_done, n.at("pT", -1))
                act.activation(probT(a), pT_ps, ACT.Copy).then_inc(pT_ready, 1)
                n.add("pT")

            def head_out(a):
                act.wait_ge(oT_done, n.at("oT", 1))
                act.activation(b_hi[:, head_kt(a), :], oT_ps[:, a % 2, :], ACT.Copy).then_inc(op_hi, 1)
                n.add("oT")

            def row_sums(src, t, out_):
                return act.activation(mem_rows[:, t, :], src[:, t, :], ACT.Square, accum_out=out_[:, t:t + 1])

            with n.loop(DEPTH, half=2 * N_UNITS, tr=TR_LAYER, acc0=ACC_LAYER, acc1=ACC_LAYER, acc2=NC,
                        head=N_HEADS, pT=N_HEADS, oT=N_HEADS, layer=1):
                split(LEAD)
                act.wait_ge(vecs_ready, n.at("layer", 1))
                chunk_done(LEAD)
                for s in range(FULL):
                    if s * HALF_KT % MEM_KT == 0:
                        act.wait_ge(mem_loaded[s * HALF_KT // MEM_KT], n.at("layer", 16, 16))
                    for kt in range(s * HALF_KT, (s + 1) * HALF_KT):
                        last = act.activation(b_hi[:, kt, :], memT[:, kt, :], ACT.Copy,
                                              scale=vecs[:, V_MEM + kt:V_MEM + kt + 1])
                    last.then_inc(op_hi, 1)
                    if 1 <= s <= FULL - LEAD:
                        split(1)
                act.wait_ge(memrow_loaded, n.at("layer", 16, 16))
                row_sums(mem_rows, 0, ss_mem)
                split(1)
                row_sums(mem_rows, 1, ss_mem).then_inc(sums_done, 1)
                split(2)
                wait_taken(1)
                op_gain(a_hi, 0, V_MIX)
                split(1)
                act.wait_ge(sums_done, n.at("layer", 1, 2 + NC))
                row_sums(x, 0, ss_x)
                split(1)
                op_gain(a_hi, 4, V_MIX)
                split(1)
                row_sums(x, 1, ss_x).then_inc(sums_done, 1)
                split(1)
                op_gain(a_hi, 8, V_MIX)
                split(1)
                n.add("acc0")
                split(1)
                op_gain(a_hi, 12, V_MIX)
                split(4)
                turn_out(mem_kT[:, :, :], vecs[:, V_MK:V_MK + 1])
                split(3)
                n.add("acc1")
                split(4)
                act.wait_ge(rs_ready, n.at("layer", 1, 2))
                take_out(0, R_U, ACT.Gelu)
                split(4)
                split(4)
                take_out(1, R_V, ACT.Gelu)
                split(4)
                n.add("acc0")
                split(5)
                op_plain(b_hi[:, 0:SGU_G, :])
                split(3)
                n.add("acc1")
                split(6)
                turn_out(kT[:, :, :], blocks=N_KV)
                split(2)
                turn_out(mem_qT[:, :, :], vecs[:, V_MQ:V_MQ + 1])
                split(4)
                take_out(0, R_Q, ACT.Copy)
                split(4)
                for s in range((NC + 1) * FULL):
                    split(1)
                    if s == 2:
                        turn_out(qT[:, 0:4, :])
                    if s == 3:
                        take_out(1, R_Q + 1, ACT.Copy)
                    if s == 10:
                        turn_out(qT[:, 4:8, :])
                    if s % 2 == 0 and 0 <= (s - 8) // 2 < N_HEADS:
                        head_exp((s - 8) // 2)
                    if s % 2 == 1 and 0 <= (s - 11) // 2 < N_HEADS:
                        head_pT((s - 11) // 2)
                    if s % 2 == 1 and 0 <= (s - 13) // 2 < N_HEADS:
                        head_out((s - 13) // 2)
                n.add("acc0", NC // 2)
                n.add("acc1", NC // 2)

                def gates(c):
                    split(5)
                    wait_taken(0)
                    act.activation(rows[:, R_U, :, :], rows[:, R_U, :, :], ACT.Sigmoid)
                    act.activation(y_rows[:, :, columns(c)], y_rows[:, :, columns(c)], ACT.Sigmoid
                                   ).then_inc(sig_ready, 1)
                    split(7)
                    wait_taken(1)
                    act.activation(rows[:, R_V, :, :], rows[:, R_V, :, :], ACT.Sigmoid).then_inc(sig_ready, 1)
                    n.add("acc0")
                    n.add("acc1")
                    n.add("acc2")

                with n.loop(NC - 1, half=HALVES_Y, acc0=2, acc1=2, acc2=1) as c:
                    gates(c)
                    split(12)
                gates(NC - 1)
                split(2)
                op_plain(b_hi[:, 0:4, :])
                split(2)
                op_plain(b_hi[:, 4:8, :])
                split(2)
                op_plain(b_hi[:, 8:12, :])
                split(5)
                op_plain(b_hi[:, 12:16, :])
                split(1)

                def x_ready(c):
                    split(5)
                    wait_taken(c % 2)
                    for t in range(TB):
                        last = act.activation(rows[:, R_Q, t, :], x[:, t, columns(c)], ACT.Square,
                                              accum_out=ss_ffn[:, t, c:c + 1])
                    last.then_inc(sums_done, 1)
                    split(1)
                    op_gain(a_hi, 4 * c, V_FFN)
                    split(2)

                for c in range(NC):
                    x_ready(c)

                def sigmoid_inner():
                    chunk_done(4)
                    for t in range(TB):
                        last = act.activation(rows[:, R_U, t, :], acc[0][:, t, :], ACT.Sigmoid,
                                              scale=rs_ffn[:, t:t + 1])
                    last.then_inc(sig_ready, 1)
                    n.add("acc0")

                def inner(groups):
                    with n.loop(groups - 1, half=2 * FULL, acc0=1, acc1=1, tr=1) as j:
                        split(4)
                        sigmoid_inner()
                        split(4)
                        n.add("acc1")
                        split(6)
                        op_plain(b_hi[:, kts(j), :])
                        split(2)
                    split(4)
                    sigmoid_inner()
                    split(4)

                def down(groups):
                    split(6)
                    op_plain(b_hi[:, kts(groups - 1), :])
                    split(2 * groups * NC - 6)
                    n.add("acc0", 2)
                    n.add("acc1", 2)

                act.wait_ge(rs_ready, n.at("layer", 2, 2))
                with n.loop(2, half=2 * PART * FULL + NC * 2 * PART, acc0=PART + 2, acc1=PART + 2, tr=PART):
                    inner(PART)
                    down(PART)
                    n.add("acc1")
                    split(FULL)
                inner(LAST)
                down(LAST)
                n.add("layer")

        @block.vector
        def _(dve):
            n = Counts(dve)
            dve.sem_inc(lo_ready, 2 * RAW_SLOTS)
            for s in (*taken, tr_free, scored):
                dve.sem_inc(s, 1)
            dve.sem_inc(bias_used, 2)

            def split(halves):
                for _ in range(halves):
                    h = n.n.get("half", 0)
                    slot, part = h // 2 % RAW_SLOTS, h % 2
                    dve.wait_ge(hi_ready, n.at("half", 1))
                    dve.tensor_tensor(w_lo[:, h % SPLIT_SLOTS, :], raw[:, slot, part * HALF:(part + 1) * HALF],
                                      w_hi[:, h % SPLIT_SLOTS, :].bitcast(F32), ALU.subtract).then_inc(lo_ready, 1)
                    n.add("half")

            def chunk_done(lead=4):
                dve.wait_ge(half_used, n.at("half", SPLIT_SLOTS - lead))

            def wait_hi():
                n.add("op")
                dve.wait_ge(op_hi, n.at("op"))

            def op_gain(hi, lo, kt0, gain):
                wait_hi()
                for k in range(kt0, kt0 + 4):
                    last = dve.scalar_tensor_tensor(out=lo[:, k, :], in0=tr[:, k - kt0, :],
                                                    scalar=vecs[:, gain + k:gain + k + 1],
                                                    in1=hi[:, k, :].bitcast(F32), op0=ALU.mult, op1=ALU.subtract)
                last.then_inc(tr_free, 1)

            def op_plain(kt):
                wait_hi()
                dve.tensor_tensor(b_lo[:, kt, :], tr[:, :, :], b_hi[:, kt, :].bitcast(F32), ALU.subtract
                                  ).then_inc(tr_free, 1)

            def rsqrt(out_, sums, width, times=None):
                m = out_.shape[-1]
                v, g, b = newton[:, 0:m], out_, guess[:, 0:m]
                dve.tensor_scalar(v, sums, 1.0 / width, EPS, ALU.mult, ALU.add)
                dve.drain()
                dve.tensor_scalar(b.bitcast(I32), v.bitcast(I32), 1, None, ALU.logical_shift_right)
                dve.drain()
                dve.tensor_scalar(g.bitcast(I32), b.bitcast(I32), -1.0, SEED, ALU.mult, ALU.add)
                for _ in range(3):
                    dve.drain()
                    dve.scalar_tensor_tensor(out=b, in0=g, scalar=-0.5, in1=g, op0=ALU.mult, op1=ALU.mult)
                    dve.drain()
                    dve.tensor_tensor(b, b, v, ALU.mult)
                    dve.drain()
                    last = dve.scalar_tensor_tensor(out=g, in0=b, scalar=1.5, in1=g, op0=ALU.add, op1=ALU.mult)
                if times is not None:
                    dve.drain()
                    last = dve.tensor_scalar(g, g, times, None, ALU.mult)
                return last

            def by_head(r, heads=4):
                return rows[:, r, :, 0:heads * HD].rearrange("p t (h d) -> p t h d", h=heads)

            def head_sums(r, tmp, heads=4):
                dve.tensor_tensor(by_head(tmp, heads), by_head(r, heads), by_head(r, heads), ALU.mult)
                dve.drain()
                dve.tensor_reduce(ss[:, 0:TB * heads].rearrange("p (t h) -> p t h", h=heads), by_head(tmp, heads),
                                  AX_X, ALU.add)
                dve.drain()

            def head_norm(r, heads=4):
                by = rs[:, 0:TB * heads].rearrange("p (t h) -> p t h", h=heads).unsqueeze(3)
                return dve.tensor_tensor(by_head(r, heads), by_head(r, heads),
                                         by.to_broadcast([P, TB, heads, HD]), ALU.mult)

            def rotate(r, tmp, tmp2, which, heads, blocks=range(TB)):
                for t in blocks:
                    src = rows[:, r, t, 0:heads * HD]
                    dst = rows[:, tmp2, t, 0:heads * HD].rearrange("p (h a f i) -> p h a f i", h=heads, a=2, f=2)
                    parts = src.rearrange("p (h a f i) -> p h a f i", h=heads, a=2, f=2)
                    dve.tensor_tensor(rows[:, tmp, t, 0:heads * HD].rearrange("p (h d) -> p h d", h=heads),
                                      src.rearrange("p (h d) -> p h d", h=heads),
                                      turn[:, which, t, :].unsqueeze(1).to_broadcast([P, heads, HD]), ALU.mult)
                    sin = turn[:, which + 1, t, :].rearrange("p (a f i) -> p a f i", a=2, f=2)
                    for f in range(2):
                        dve.tensor_tensor(dst[:, :, :, f, :], parts[:, :, :, 1 - f, :],
                                          sin[:, :, f, :].unsqueeze(1).to_broadcast([P, heads, 2, HD // 4]),
                                          ALU.mult)
                dve.drain()
                for t in blocks:
                    last = dve.tensor_tensor(rows[:, r, t, 0:heads * HD], rows[:, tmp, t, 0:heads * HD],
                                             rows[:, tmp2, t, 0:heads * HD], ALU.add)
                return last

            def take_scaled(acc_i, dst, factor):
                chunk_done()
                for t in range(TB):
                    last = dve.tensor_scalar(dst[:, t, :], acc[acc_i][:, t, :], factor[:, t:t + 1], None, ALU.mult)
                last.then_inc(taken[acc_i], 1)
                n.add(f"acc{acc_i}")

            def take_gate(acc_i, dst, k, lead=4):
                chunk_done(lead)
                dve.wait_ge(bias_loaded[k % 2], n.at(f"bias{k % 2}", 16, 16))
                for t in range(TB):
                    last = dve.scalar_tensor_tensor(out=dst[:, t, :], in0=acc[acc_i][:, t, :],
                                                    scalar=rs_x[:, t:t + 1], in1=bias[:, k % 2, :],
                                                    op0=ALU.mult, op1=ALU.add)
                last.then_inc(taken[acc_i], 1)
                dve.drain().then_inc(bias_used, 1)
                n.add(f"acc{acc_i}")
                n.add(f"bias{k % 2}")

            def take_x(acc_i, c):
                xc = x[:, :, columns(c)]
                last = dve.tensor_tensor(xc, acc[acc_i][:, :, :], xc, ALU.add)
                n.add(f"acc{acc_i}")
                return last

            def wait_taken(acc_i):
                n.add(f"acc{acc_i}")
                dve.wait_ge(taken[acc_i], n.at(f"acc{acc_i}", 1))

            def head_max(a):
                dve.wait_ge(scored, n.at("head", 2))
                dve.tensor_reduce(top[:, a % 2, :], scores[:, a % 2, :].rearrange("p (t k) -> p t k", t=TB),
                                  AX_X, ALU.max)
                dve.drain()
                dve.scalar_tensor_tensor(out=low[:, a % 2, :], in0=top[:, a % 2, :], scalar=-1.0,
                                         in1=q_scale[:, a // 4, :, a % 4], op0=ALU.mult, op1=ALU.mult
                                         ).then_inc(low_ready, 1)
                n.add("head")

            def head_inv(a):
                dve.wait_ge(exp_done, n.at("inv", 1))
                dve.reciprocal(inv[:, a % 2, :], den[:, a % 2, :]).then_inc(inv_ready, 1)
                n.add("inv")

            def head_out(a):
                wait_hi()
                dve.tensor_tensor(b_lo[:, head_kt(a), :], oT_ps[:, a % 2, :], b_hi[:, head_kt(a), :].bitcast(F32),
                                  ALU.subtract).then_inc(head_ready, 1)

            dve.wait_ge(vecs_loaded, 16)
            with n.loop(DEPTH, half=2 * N_UNITS, op=OPS_LAYER, acc0=ACC_LAYER, acc1=ACC_LAYER, acc2=NC,
                        head=N_HEADS, inv=N_HEADS, sums=2 + NC, sig=SIG_LAYER, bias0=N_BRANCH * NC // 2,
                        bias1=N_BRANCH * NC // 2, layer=1) as layer:
                dve.tensor_copy(vecs[:, :], vecs_all[:, layer, :]).then_inc(vecs_ready, 1)
                split(LEAD)
                for s in range(FULL):
                    wait_hi()
                    for kt in range(s * HALF_KT, (s + 1) * HALF_KT):
                        last = dve.scalar_tensor_tensor(out=b_lo[:, kt, :], in0=memT[:, kt, :],
                                                        scalar=vecs[:, V_MEM + kt:V_MEM + kt + 1],
                                                        in1=b_hi[:, kt, :].bitcast(F32), op0=ALU.mult,
                                                        op1=ALU.subtract)
                    last.then_inc(mem_ready, 1)
                    if s == 3:
                        dve.wait_ge(x_loaded, 16)
                        take_x(1, NC - 1).then_inc(taken[1], 1)
                    if 1 <= s <= FULL - LEAD:
                        split(1)
                split(1)
                n.add("sums")
                dve.wait_ge(sums_done, n.at("sums"))
                rsqrt(rs_mem, ss_mem, D)
                dve.drain()
                split(2)
                op_gain(a_hi, a_lo, 0, V_MIX)
                split(1)
                take_scaled(0, rows[:, R_MK, :, :], rs_mem)
                dve.drain()
                split(1)
                op_gain(a_hi, a_lo, 4, V_MIX)
                split(1)
                head_sums(R_MK, R_TMP)
                split(1)
                op_gain(a_hi, a_lo, 8, V_MIX)
                split(1)
                rsqrt(rs[:, 0:8], ss[:, 0:8], HD)
                dve.drain()
                head_norm(R_MK).then_inc(rows_ready, 1)
                split(1)
                op_gain(a_hi, a_lo, 12, V_MIX)
                split(1)
                n.add("sums")
                dve.wait_ge(sums_done, n.at("sums"))
                rsqrt(rs_x, ss_x, D).then_inc(rs_ready, 1)
                split(2)
                take_scaled(1, mem_v[:, :, :], rs_mem)
                split(1)
                dve.wait_ge(rope_loaded, 16)
                dve.wait_ge(layer_loaded, n.at("layer", 32, 32))
                for i, g in ((0, 1), (2, 2)):
                    gain = gains[:, g * HD:(g + 1) * HD]
                    dve.tensor_tensor(turn[:, i, :, :], rope[:, 0, :, :],
                                      gain.unsqueeze(1).to_broadcast([P, TB, HD]), ALU.mult)
                    swap = gain.rearrange("p (a f i) -> p a f i", a=2, f=2)
                    sin = rope[:, 1, :, :].rearrange("p t (a f i) -> p t a f i", a=2, f=2)
                    to = turn[:, i + 1, :, :].rearrange("p t (a f i) -> p t a f i", a=2, f=2)
                    for t in range(TB):
                        for f in range(2):
                            dve.tensor_tensor(to[:, t, :, f, :], sin[:, t, :, f, :], swap[:, :, 1 - f, :], ALU.mult)
                split(3)
                split(FULL)
                wait_taken(0)
                split(5)
                wait_taken(1)
                head_sums(R_V, R_TMP)
                split(1)
                rsqrt(rs[:, 0:8], ss[:, 0:8], HD)
                dve.drain()
                split(1)
                for t in range(TB):
                    for g in range(SGU_G):
                        v_ = rows[:, R_V, t, g * HD:(g + 1) * HD]
                        last = dve.scalar_tensor_tensor(out=v_, in0=v_, scalar=rs[:, 4 * t + g:4 * t + g + 1],
                                                        in1=gains[:, 0:HD], op0=ALU.mult, op1=ALU.mult)
                last.then_inc(rows_ready, 1)
                split(1)
                split(2)
                dve.wait_ge(sgu_done, n.at("layer", 1))
                for g in range(SGU_G):
                    u_ = rows[:, R_U, :, g * HD:(g + 1) * HD]
                    sp_ = acc[2][:, g // 2, g % 2 * SEQ:(g % 2 + 1) * SEQ].rearrange("p (t d) -> p t d", t=TB)
                    last = dve.scalar_tensor_tensor(out=u_, in0=sp_, scalar=vecs[:, V_SGUB + g:V_SGUB + g + 1],
                                                    in1=u_, op0=ALU.add, op1=ALU.mult)
                last.then_inc(rows_ready, 1)
                split(2)
                take_scaled(0, rows[:, R_KV, :, :], rs_x)
                dve.drain()
                split(1)
                op_plain(slice(0, SGU_G))
                head_sums(R_KV, R_V, N_KV)
                split(1)
                rsqrt(rs[:, 0:TB * N_KV], ss[:, 0:TB * N_KV], HD)
                dve.drain()
                head_norm(R_KV, N_KV)
                dve.drain()
                split(1)
                rotate(R_KV, R_V, R_Q, 2, N_KV).then_inc(rows_ready, 1)
                split(1)
                split(4)
                take_scaled(1, rows[:, R_MQ, :, :], rs_x)
                dve.drain()
                split(1)
                head_sums(R_MQ, R_V)
                split(1)
                rsqrt(q_scale[:, 0, :, :].rearrange("p t h -> p (t h)"), ss[:, 0:8], HD, SCALE)
                split(2)
                split(5)
                wait_taken(0)
                head_sums(R_Q, R_V)
                split(1)
                rsqrt(q_scale[:, 1, :, :].rearrange("p t h -> p (t h)"), ss[:, 0:8], HD, SCALE)
                split(1)
                rotate(R_Q, R_V, R_TMP, 0, 4).then_inc(rows_ready, 1)
                split(1)
                for s in range((NC + 1) * FULL):
                    split(1)
                    if s == 4:
                        wait_taken(1)
                        head_sums(R_Q + 1, R_V)
                    if s == 5:
                        rsqrt(q_scale[:, 2, :, :].rearrange("p t h -> p (t h)"), ss[:, 0:8], HD, SCALE)
                    if s == 6:
                        rotate(R_Q + 1, R_V, R_Q, 0, 4).then_inc(rows_ready, 1)
                    if s >= FULL + 3 and s % FULL == 3:
                        c = s // FULL - 1
                        take_gate(c % 2, y_rows[:, :, columns(c)], c)
                    if s % 2 == 1 and 0 <= (s - 7) // 2 < N_HEADS:
                        head_max((s - 7) // 2)
                    if s % 2 == 1 and 0 <= (s - 9) // 2 < N_HEADS:
                        head_inv((s - 9) // 2)
                    if s % 2 == 1 and 0 <= (s - 13) // 2 < N_HEADS:
                        head_out((s - 13) // 2)

                def wait_sig():
                    n.add("sig")
                    dve.wait_ge(sig_ready, n.at("sig"))

                def gates(c):
                    yc = y_rows[:, :, columns(c)]
                    split(4)
                    take_gate(0, rows[:, R_U, :, :], 4)
                    split(7)
                    take_gate(1, rows[:, R_V, :, :], 5, lead=3)
                    split(3)
                    wait_sig()
                    dve.tensor_tensor(yc, yc, acc[0][:, :, :], ALU.mult).then_inc(taken[0], 1)
                    n.add("acc0")

                def branch(acc_i, r, c):
                    yc = y_rows[:, :, columns(c)]
                    dve.tensor_tensor(rows[:, r, :, :], rows[:, r, :, :], acc[acc_i][:, :, :], ALU.mult
                                      ).then_inc(taken[acc_i], 1)
                    n.add(f"acc{acc_i}")
                    dve.drain()
                    return dve.tensor_tensor(yc, yc, rows[:, r, :, :], ALU.add)

                with n.loop(NC - 1, half=HALVES_Y, acc0=2, acc1=2, acc2=1, sig=2, bias0=1, bias1=1) as c:
                    gates(c)
                    split(2)
                    wait_sig()
                    branch(1, R_V, c)
                    split(4)
                    chunk_done()
                    branch(2, R_U, c).then_inc(rows_ready, 1)
                    split(4)
                c = NC - 1
                gates(c)
                op_plain(slice(0, 4))
                split(2)
                wait_sig()
                branch(1, R_V, c)
                op_plain(slice(4, 8))
                split(2)
                op_plain(slice(8, 12))
                split(2)
                chunk_done()
                branch(2, R_U, c).then_inc(rows_ready, 1)
                split(3)
                op_plain(slice(12, 16))
                split(1)
                for c in range(NC):
                    split(4)
                    chunk_done()
                    take_x(c % 2, c).then_inc(taken[c % 2], 1)
                    split(2)
                    op_gain(a_hi, a_lo, 4 * c, V_FFN)
                    n.add("sums")
                    if c == NC - 1:
                        split(1)
                        dve.wait_ge(sums_done, n.at("sums"))
                        dve.tensor_reduce(ss_sum, ss_ffn, AX_X, ALU.add)
                        dve.drain()
                        rsqrt(rs_ffn, ss_sum, D).then_inc(rs_ready, 1)
                        split(1)
                    else:
                        split(2)

                def take_inner(acc_i, r):
                    for t in range(TB):
                        last = dve.scalar_tensor_tensor(out=rows[:, r, t, :], in0=acc[acc_i][:, t, :],
                                                        scalar=rs_ffn[:, t:t + 1], in1=rows[:, R_U, t, :],
                                                        op0=ALU.mult, op1=ALU.mult)
                    last.then_inc(taken[acc_i], 1)
                    n.add(f"acc{acc_i}")

                def gate_inner():
                    split(5)
                    wait_sig()
                    take_inner(0, R_U)
                    split(3)

                def inner(groups):
                    with n.loop(groups - 1, half=2 * FULL, acc0=1, acc1=1, op=1, sig=1) as j:
                        gate_inner()
                        split(4)
                        chunk_done()
                        take_inner(1, R_MQ)
                        split(2)
                        op_plain(kts(j))
                        split(2)
                    gate_inner()

                def down(groups):
                    split(4)
                    chunk_done()
                    take_inner(1, R_MQ)
                    split(2)
                    op_plain(kts(groups - 1))
                    split(2 * groups - 6)
                    for c in range(1, NC):
                        split(4)
                        chunk_done()
                        take_x((c - 1) % 2, c - 1).then_inc(taken[(c - 1) % 2], 1)
                        split(2 * groups - 4)

                with n.loop(2, half=2 * PART * FULL + NC * 2 * PART, acc0=PART + 2, acc1=PART + 2, op=PART,
                            sig=PART):
                    inner(PART)
                    down(PART)
                    split(4)
                    chunk_done()
                    take_x(1, NC - 1).then_inc(taken[1], 1)
                    split(4)
                inner(LAST)
                down(LAST)
                n.add("layer")
            chunk_done(0)
            take_x(1, NC - 1).then_inc(x_final, 1)


TR_Y = NC + 6 + NC
TR_LAYER = TR_Y + NC + ACT_GROUPS
ROWS_LAYER = 6 + NC
HALVES_Y = 2 * FULL + 2 + 2 + 4
ACC_LAYER = 1 + 3 + NC // 2 + (1 + 2 * (NC - 1) + 1) + NC // 2 + (PART + 2) * 2 + 1 + LAST - 1 + 2
SIG_LAYER = 2 * NC + ACT_GROUPS


def rope_tables():
    half = HD // 2
    inv = np.float32(ROPE_THETA) ** (-np.arange(0, half, 2, dtype=np.float32) / np.float32(half))
    pos = np.arange(SEQ)
    ar = (pos // GRID_W).astype(np.float32)[:, None] * inv[None, :]
    ac = (pos % GRID_W).astype(np.float32)[:, None] * inv[None, :]
    cos = np.concatenate([np.cos(ar), np.cos(ar), np.cos(ac), np.cos(ac)], axis=1)
    sin = np.concatenate([-np.sin(ar), np.sin(ar), -np.sin(ac), np.sin(ac)], axis=1)
    both = np.stack([cos, sin]).astype(np.float32).reshape(2, TB, P, HD)
    return np.ascontiguousarray(both.transpose(2, 0, 1, 3))


def kernel(x, mem, norm_mix, w_in, gate_b, sgu_norm, sgu_w, sgu_b, q_norm, k_norm, mem_norm, w_mem_kv,
           mq_norm, mk_norm, w_br_sgu, w_br_attn, w_br_mem, w_out, norm_ffn, w_gate_up, w_down):
    import concourse.bacc as bacc
    from concourse.bass_utils import run_bass_kernel_spmd

    def per_feature(v):
        return np.asarray(v).reshape(-1, P).T

    stream = np.empty((DEPTH, N_UNITS, P, UNIT), np.float32)
    vecs = np.empty((P, DEPTH, N_VEC), np.float32)
    for l in range(DEPTH):
        at = 0
        for w, c in layer_stream(*(np.asarray(w[l]) for w in (w_in, w_mem_kv, w_br_sgu, w_br_attn, w_br_mem,
                                                             w_out, w_gate_up, w_down))):
            u = units_of(w, c)
            stream[l, at:at + len(u)] = u
            at += len(u)
        assert at == N_UNITS
        vecs[:, l] = np.concatenate([per_feature(v[l]) for v in (mem_norm, norm_mix, norm_ffn, mq_norm, mk_norm,
                                                                 sgu_b)], axis=1)
    gb = np.asarray(gate_b).reshape(DEPTH, N_BRANCH, NC, COLS)
    bias = np.concatenate([gb[:, 0], np.stack([gb[:, 1], gb[:, 2]], axis=2).reshape(DEPTH, 2 * NC, COLS)], axis=1)
    arrays = {
        "weights": stream,
        "x_in": np.asarray(x),
        "mem_in": np.asarray(mem),
        "memT_in": np.asarray(mem)[0].T.reshape(KT, P, SEQ).transpose(1, 0, 2),
        "vecs_in": vecs,
        "gains_in": np.concatenate([np.asarray(v) for v in (sgu_norm, q_norm, k_norm)], axis=1)[:, None, :],
        "sguT_in": np.asarray(sgu_w).transpose(0, 3, 1, 2).reshape(DEPTH, P, SGU_G * P),
        "rope_in": rope_tables(),
        "bias_in": bias,
    }
    nc = bacc.Bacc("TRN2", target_bir_lowering=False, num_devices=1,
                   dynamic_dma_scratch_size=DMA_RING)
    arrays = {name: np.ascontiguousarray(a) for name, a in arrays.items()}
    args = [nc.dram_tensor(name, a.shape, F32, kind="ExternalInput").ap() for name, a in arrays.items()]
    out = nc.dram_tensor("out", tuple(np.shape(x)), F32, kind="ExternalOutput").ap()
    trunk(nc, *args, out)
    got = run_bass_kernel_spmd(nc, [arrays], core_ids=[0])
    return got.results[0]["out"]
```
